# Optimizing a Trainium2 kernel written in Bass

```python
import jax, jax.numpy as jnp
from jax import lax
import numpy as np

D_MODEL = 1024
BATCH = 1
SEQ = 256
DEPTH = 2

CHUNK = 64
QBLOCK = 128
HG_HEADS = 4
HG_DK = 128
HG_DV = 128
HG_WIDTH = HG_HEADS * HG_DK
SA_HEADS = 8
SA_DH = 64
SA_WIDTH = SA_HEADS * SA_DH
SA_LATENT = 128
IDX_HEADS = 4
IDX_DIM = 64
TOPK_MAX = 256
SB_HEADS = 8
SB_DH = 64
SB_WIDTH = SB_HEADS * SB_DH
N_BRANCH = 3
BRANCH_WIDTH = 512
D_FF = 2816
N_EXPERTS = 8
TOP_K_EXPERTS = 2
D_FF_EXPERT = 2816
N_DENSE = (DEPTH + 1) // 2
N_MOE = DEPTH // 2
PLE_DIM = 256
EPS = 1e-6
IN_SPLITS = (HG_WIDTH, HG_WIDTH, HG_HEADS * HG_DV, HG_HEADS * HG_DV,
             SA_WIDTH, SA_LATENT, IDX_HEADS * IDX_DIM, IDX_DIM, IDX_HEADS,
             SB_WIDTH, SB_WIDTH, SB_WIDTH, N_BRANCH * D_MODEL)
IN_WIDTH = sum(IN_SPLITS)

kernel_name = "hybrid_hgrn2_dsa_stickbreak_moe_block"

F32 = jnp.float32

def rmsnorm(x, g):
    xf = x.astype(F32)
    y = xf * lax.rsqrt(jnp.mean(xf * xf, axis=-1, keepdims=True) + EPS)
    return (y * g.astype(F32)).astype(x.dtype)

def hgrn2_mixer(q_in, f_in, i_in, g_in, lb, onorm):
    B, S, _ = q_in.shape
    nC = S // CHUNK
    lbf = lb.astype(F32)
    fpre = f_in.astype(F32)
    q = jax.nn.silu(q_in.astype(F32))
    log_f = jnp.log(lbf + (1.0 - lbf) * jax.nn.sigmoid(fpre))
    k = (1.0 - lbf) * jax.nn.sigmoid(-fpre)
    v = i_in.astype(F32)

    def to_chunks(t, d):
        return t.reshape(B, nC, CHUNK, HG_HEADS, d).transpose(1, 0, 3, 2, 4)

    causal = jnp.tril(jnp.ones((CHUNK, CHUNK), dtype=bool))[None, None, :, :, None]

    def step(state, inp):
        qc, kc, vc, lfc = inp
        b = jnp.cumsum(lfc, axis=2)
        diff = b[:, :, :, None, :] - b[:, :, None, :, :]
        decay = jnp.exp(jnp.where(causal, diff, -jnp.inf))
        scores = jnp.einsum('bhtd,bhsd,bhtsd->bhts', qc, kc, decay)
        o = jnp.einsum('bhts,bhsv->bhtv', scores, vc) + \
            jnp.einsum('bhtd,bhdv->bhtv', qc * jnp.exp(b), state)
        b_last = b[:, :, -1:, :]
        state = jnp.exp(b_last[:, :, 0, :])[..., None] * state + \
            jnp.einsum('bhsd,bhsv->bhdv', kc * jnp.exp(b_last - b), vc)
        return state, o

    state0 = jnp.zeros((B, HG_HEADS, HG_DK, HG_DV), F32)
    _, o = lax.scan(step, state0, (to_chunks(q, HG_DK), to_chunks(k, HG_DK),
                                   to_chunks(v, HG_DV), to_chunks(log_f, HG_DK)))
    o = o.transpose(1, 0, 3, 2, 4).reshape(B, S, HG_HEADS, HG_DV)
    o = rmsnorm(o, onorm).reshape(B, S, HG_HEADS * HG_DV)
    o = o * jax.nn.silu(g_in.astype(F32))
    return o.astype(q_in.dtype)

def dsa_mixer(q_in, c_in, iq_in, ik_in, iw_in, cnorm, wk, wv):
    B, S, _ = q_in.shape
    nb = S // QBLOCK
    topk = min(TOPK_MAX, S // 4)
    c = rmsnorm(c_in, cnorm)
    k = c @ wk
    v = c @ wv
    q = q_in.reshape(B, S, SA_HEADS, SA_DH)
    iq = iq_in.reshape(B, S, IDX_HEADS, IDX_DIM)
    ik = ik_in.astype(F32)
    iw = iw_in * (IDX_HEADS ** -0.5)
    kchunk = jnp.arange(S) // CHUNK
    gather = jax.vmap(lambda t, idx: t[idx])

    def blocks(t):
        return t.reshape((B, nb, QBLOCK) + t.shape[2:]).swapaxes(0, 1)

    def attend(blk):
        qb, iqb, iwb, qchunk = blk
        isc = jnp.einsum('bthd,bsd->bths', iqb.astype(F32), ik)
        isc = jnp.einsum('bths,bth->bts', jax.nn.relu(isc), iwb.astype(F32))
        adm = kchunk[None, :] <= qchunk[:, None]
        isc = jnp.where(adm[None], isc, -jnp.inf)
        _, sel = lax.top_k(isc, topk)
        valid = kchunk[sel] <= qchunk[None, :, None]
        k_sel = gather(k, sel).astype(F32)
        v_sel = gather(v, sel).astype(F32)
        logits = jnp.einsum('bthd,btkd->bthk', qb.astype(F32), k_sel) * (SA_DH ** -0.5)
        logits = jnp.where(valid[:, :, None, :], logits, -jnp.inf)
        w = jax.nn.softmax(logits, axis=-1)
        return jnp.einsum('bthk,btkd->bthd', w, v_sel)

    qchunks = (jnp.arange(S) // CHUNK).reshape(nb, QBLOCK)
    o = lax.map(attend, (blocks(q), blocks(iq), blocks(iw), qchunks))
    o = o.swapaxes(0, 1).reshape(B, S, SA_WIDTH)
    return o.astype(q_in.dtype)

def stick_breaking_mixer(q_in, k_in, v_in):
    B, S, _ = q_in.shape
    q = q_in.reshape(B, S, SB_HEADS, SB_DH).astype(F32)
    k = k_in.reshape(B, S, SB_HEADS, SB_DH).astype(F32)
    v = v_in.reshape(B, S, SB_HEADS, SB_DH).astype(F32)
    scale = SB_DH ** -0.5
    outs = []
    for j in range(S // QBLOCK):
        start = j * QBLOCK
        end = start + QBLOCK
        z = jnp.einsum('bthd,bshd->bhts', q[:, start:end], k[:, :end]) * scale
        t_pos = start + jnp.arange(QBLOCK)
        s_pos = jnp.arange(end)
        strict = s_pos[None, :] < t_pos[:, None]
        log_keep = jnp.where(strict, jax.nn.log_sigmoid(-z), 0.0)
        after = lax.cumsum(log_keep, axis=3, reverse=True) - log_keep
        A = jnp.where(strict, jnp.exp(jax.nn.log_sigmoid(z) + after), 0.0)
        outs.append(jnp.einsum('bhts,bshd->bthd', A, v[:, :end]))
    o = jnp.concatenate(outs, axis=1).reshape(B, S, SB_WIDTH)
    return o.astype(q_in.dtype)

def swiglu(v, wg, wu, wd):
    return (jax.nn.silu(v @ wg) * (v @ wu)) @ wd

def moe_swiglu(v, router, wg, wu, wd):
    logits = (v @ router).astype(F32)
    top_val, top_idx = lax.top_k(logits, TOP_K_EXPERTS)
    top_w = jax.nn.softmax(top_val, axis=-1)
    combine = jnp.sum(jax.nn.one_hot(top_idx, N_EXPERTS, dtype=F32) * top_w[..., None], axis=-2)
    combine = combine.astype(v.dtype)
    y = jnp.zeros_like(v)
    for e in range(N_EXPERTS):
        y = y + combine[..., e:e + 1] * swiglu(v, wg[e], wu[e], wd[e])
    return y

def setup_inputs(seed: int = 0) -> dict:
    key = jax.random.key(seed)
    ks = jax.random.split(key, 24)
    D = D_MODEL

    def nrm(k, shape, fan_in):
        return jax.random.normal(k, shape, F32) * (fan_in ** -0.5)

    def gain(k, shape):
        return 1.0 + 0.02 * jax.random.normal(k, shape, F32)

    return {
        "x": jax.random.normal(ks[0], (BATCH, SEQ, D), F32),
        "p": jax.random.normal(ks[1], (DEPTH, BATCH, SEQ, PLE_DIM), F32),
        "lb_param": 0.1 * jax.random.normal(ks[2], (DEPTH, HG_WIDTH), F32),
        "norm_mix": gain(ks[3], (DEPTH, D)),
        "w_in": nrm(ks[4], (DEPTH, D, IN_WIDTH), D),
        "hg_onorm": gain(ks[5], (DEPTH, HG_DV)),
        "sa_cnorm": gain(ks[6], (DEPTH, SA_LATENT)),
        "sa_wk": nrm(ks[7], (DEPTH, SA_LATENT, SA_DH), SA_LATENT),
        "sa_wv": nrm(ks[8], (DEPTH, SA_LATENT, SA_DH), SA_LATENT),
        "w_branch": nrm(ks[9], (DEPTH, N_BRANCH, BRANCH_WIDTH, D), BRANCH_WIDTH),
        "w_out": nrm(ks[10], (DEPTH, D, D), D),
        "norm_ffn": gain(ks[11], (DEPTH, D)),
        "dense_wg": nrm(ks[12], (N_DENSE, D, D_FF), D),
        "dense_wu": nrm(ks[13], (N_DENSE, D, D_FF), D),
        "dense_wd": nrm(ks[14], (N_DENSE, D_FF, D), D_FF),
        "moe_router": nrm(ks[15], (N_MOE, D, N_EXPERTS), D),
        "moe_wg": nrm(ks[16], (N_MOE, N_EXPERTS, D, D_FF_EXPERT), D),
        "moe_wu": nrm(ks[17], (N_MOE, N_EXPERTS, D, D_FF_EXPERT), D),
        "moe_wd": nrm(ks[18], (N_MOE, N_EXPERTS, D_FF_EXPERT, D), D_FF_EXPERT),
        "norm_ple": gain(ks[19], (DEPTH, D)),
        "ple_gate": nrm(ks[20], (DEPTH, D, D), D),
        "ple_proj": nrm(ks[21], (DEPTH, PLE_DIM, D), PLE_DIM),
        "norm_final": gain(ks[22], (D,)),
    }

def reference(x, p, lb_param, norm_mix, w_in, hg_onorm, sa_cnorm, sa_wk, sa_wv, w_branch,
              w_out, norm_ffn, dense_wg, dense_wu, dense_wd, moe_router, moe_wg, moe_wu,
              moe_wd, norm_ple, ple_gate, ple_proj, norm_final):
    B, S, D = x.shape
    lb_sm = jax.nn.softmax(lb_param.astype(F32), axis=0)
    lb_all = jnp.cumsum(lb_sm, axis=0) - lb_sm[0:1]
    split_points = np.cumsum(np.array(IN_SPLITS))[:-1]
    h = x
    for i in range(DEPTH):
        u = rmsnorm(h, norm_mix[i])
        z = u @ w_in[i]
        (hq, hf, hi, hg, sq, sc, iq, ik, iw, bq, bk, bv, gz) = jnp.split(z, split_points, axis=-1)
        a = hgrn2_mixer(hq, hf, hi, hg, lb_all[i], hg_onorm[i])
        b = dsa_mixer(sq, sc, iq, ik, iw, sa_cnorm[i], sa_wk[i], sa_wv[i])
        c = stick_breaking_mixer(bq, bk, bv)
        branches = jnp.stack([a, b, c], axis=2)
        proj = jnp.einsum('bsnw,nwd->bsnd', branches, w_branch[i])
        gates = jax.nn.sigmoid(gz.astype(F32)).reshape(B, S, N_BRANCH, D).astype(proj.dtype)
        merged = jnp.sum(gates * proj, axis=2)
        h = h + merged @ w_out[i]
        v = rmsnorm(h, norm_ffn[i])
        if i % 2 == 0:
            j = i // 2
            h = h + swiglu(v, dense_wg[j], dense_wu[j], dense_wd[j])
        else:
            j = i // 2
            h = h + moe_swiglu(v, moe_router[j], moe_wg[j], moe_wu[j], moe_wd[j])
        ple_g = jax.nn.sigmoid((rmsnorm(h, norm_ple[i]) @ ple_gate[i]).astype(F32)).astype(h.dtype)
        h = h + ple_g * (p[i] @ ple_proj[i])
    return rmsnorm(h, norm_final)


_drawn_inputs = setup_inputs


def setup_inputs(seed=0):
    import zlib

    import numpy as np

    out = dict(_drawn_inputs(seed))
    spreads = {}
    factors = {'lb_param': 5.36,
     'hg_onorm': 3.237,
     'sa_cnorm': 3.633,
     'norm_ple': 6.096,
     'norm_final': 2.832}
    for name, (base, spread) in spreads.items():
        noise = np.random.default_rng([zlib.crc32(name.encode()), seed]).standard_normal(out[name].shape)
        drawn = base * np.exp(spread * noise) if base else spread * noise
        out[name] = __import__('jax').numpy.asarray(drawn.astype(out[name].dtype))
    for name, factor in factors.items():
        out[name] = (out[name] * factor).astype(out[name].dtype)
    return out
```

```python
import concourse.bass as bass
from concourse import mybir
from contextlib import ExitStack

P = 128
SEQ, D = 256, 1024
DEPTH = 2
NT = SEQ // P
KC = D // P
WIDTH = 512
HG_H, SA_H, SB_H, DH, IDX_H = 4, 8, 8, 64, 4
TOPK = 64
FF = 2816
FS = 256
NS = FF // FS
NE = 8
PLE = 256
EPS = 1e-6
SCALE = DH ** -0.5
GRAN = 4 * 512
RAW = 4
RAW_MOE = 6
WR = 3

REPLACED = -3.0e38
MASKED = -1.0e30

COLS = dict(bq=3012, bk=3524, bv=4036, sq=2048, sx=2560, hq=0, hf=512, hi=1024, hg=1536, gz=4548)
SLICES = [(COLS[n], 452 if n == "sx" else 512) for n in ("bq", "bk", "bv", "sq", "sx", "hq", "hf", "hi", "hg")]
BRANCHES = (2, 1, 0)
SLICES += [(COLS["gz"] + n * D + half * 512, 512) for n in BRANCHES for half in range(2)]
NZ = len(SLICES)

G_BR = 2 * NZ
G_OUT = G_BR + 6
G_FF = G_OUT + 4
G_PLE0 = G_FF + 3 * NS
L1 = G_PLE0 + 5
M0 = L1 + G_FF
PER_E = 3 * NS
N_MOE = NE * PER_E


def build(nc, x, p, lb_param, norm_mix, w_in, hg_onorm, sa_cnorm, sa_wk, sa_wv, w_branch, w_out,
          norm_ffn, dense_wg, dense_wu, dense_wd, moe_router, moe_wg, moe_wu, moe_wd, norm_ple,
          ple_gate, ple_proj, norm_final, out):
    f32, f32r, i32, u32, u8 = (mybir.dt.float32, mybir.dt.float32r, mybir.dt.int32, mybir.dt.uint32,
                               mybir.dt.uint8)
    ALU, ACT, AX = mybir.AluOpType, mybir.ActivationFunctionType, mybir.AxisListType
    ctx = ExitStack()
    with ctx:
        def sb(name, cols, dt=f32):
            return ctx.enter_context(nc.sbuf_tensor(name, [P, cols], dt))

        def sem(name):
            return ctx.enter_context(nc.semaphore(name))

        h = sb("h", NT * D)
        whi, wlo = sb("whi", WR * GRAN, f32r), sb("wlo", WR * GRAN, f32r)
        ahi, alo = sb("ahi", 5120, f32r), sb("alo", 5120, f32r)
        ARENA = RAW * GRAN + 18688
        arena = sb("arena", ARENA)
        ident, later, ones = sb("ident", P), sb("later", P), sb("ones", P)
        cnorm, onorm, wk2, wv2 = sb("cnorm", P), sb("onorm", P), sb("wk2", P), sb("wv2", P)
        slots_iota = sb("slots_iota", P)
        masks = sb("masks", 8 * P, u8)
        router = sb("router", KC * NE)
        lbp = sb("lbp", 2 * HG_H)
        lb, oml = sb("lb", 2 * HG_H), sb("oml", 2 * HG_H)
        lbt = sb("lbt", 4 * HG_H)
        neg_half = sb("neg_half", 8)
        small = sb("small", 105)
        psel = ahi[:, 4608:4864]
        biggest = sb("biggest", 1, i32)
        ps = ctx.enter_context(nc.psum_tensor("ps", [P, 8 * 512], f32))

        def bank(b, n=512, off=0):
            return ps[:, b * 512 + off:b * 512 + off + n]

        def raw(slot):
            return arena[:, slot * GRAN:(slot + 1) * GRAN]

        WORK = RAW * GRAN
        ZHG = WORK + 6144
        T = ZHG + 4096

        def wk(off, n):
            return arena[:, off:off + n]

        def zs(i, t, n=512):
            base = WORK + (2 * i + t) * 512 if i < 5 else ZHG + (2 * (i - 5) + t) * 512
            if i >= 9:
                base = WORK + (2 * (i - 9) + t) * 512
            return arena[:, base:base + n]

        def gate(i):
            return arena[:, WORK + 1024 * i:WORK + 1024 * i + 1024]

        def gain(r):
            return wk(ZHG + (0 if r % 2 == 0 else 3072), D)

        def u_nat(t):
            return wk(ZHG + 1024 + t * D, D)

        ss, rstd = small[:, 0:2], small[:, 2:4]
        css, crstd = small[:, 4:6], small[:, 6:8]
        hss, hrstd = small[:, 8:16], small[:, 16:24]
        mx, nmx = small[:, 24:40], small[:, 40:56]
        sums, rsums = small[:, 56:72], small[:, 72:88]
        top8, iwh, zero = small[:, 88:96], small[:, 96:104], small[:, 104:105]

        consts, x_landed, p_landed, layer_consts = sem("consts"), sem("x_landed"), sem("p_landed"), sem("layer_consts")
        gain_landed = [sem("gain_landed0"), sem("gain_landed1")]
        landed = [sem(f"raw_landed{i}") for i in range(RAW)]
        moe_landed = [sem(f"moe_raw_landed{i}") for i in range(RAW_MOE)]
        pool_consts, pool_chain, dve_chain = sem("pool_consts"), sem("pool_chain"), sem("dve_chain")
        lb_shifted, lb_exp, lb_done = sem("lb_shifted"), sem("lb_exp"), sem("lb_done")
        hi_ready, lo_ready, gemm_done = sem("hi_ready"), sem("lo_ready"), sem("gemm_done")
        lo_pool = sem("lo_ready_pool")
        acc_out_act, acc_out_dve = sem("acc_out_act"), sem("acc_out_dve")
        squares, rstd_ready, u_ready = sem("squares"), sem("rstd_ready"), sem("u_ready")
        at_ready, at_hi, at_lo = sem("aT_ready"), sem("aT_hi"), sem("aT_lo")
        ffn_added, ple_added, merged_ready = sem("ffn_added"), sem("ple_added"), sem("merged_ready")
        pe_step, act_step, dve_step = sem("pe_step"), sem("act_step"), sem("dve_step")
        even_heads = sem("even_heads")
        sb_sig, sb_masked = sem("sb_sig"), sem("sb_masked")
        c_squares, c_rstd, c_ready = sem("c_squares"), sem("c_rstd"), sem("c_ready")
        sa_relu, sa_neg_max, sa_exp = sem("sa_relu"), sem("sa_neg_max"), sem("sa_exp")
        hg_sig, hg_gsig, hg_gs, hg_x = sem("hg_sig"), sem("hg_gsig"), sem("hg_gs"), sem("hg_x")
        hg_ss, hg_rstd = sem("hg_ss"), sem("hg_rstd")
        d_silu, d_ff, d_tr, d_thi, d_tlo = (sem("dense_silu"), sem("dense_ff"), sem("dense_ffT"),
                                            sem("dense_ffT_hi"), sem("dense_ffT_lo"))
        pt_ready, pt_hi, pt_lo = sem("pT_ready"), sem("pT_hi"), sem("pT_lo")
        v_hi, v_lo, vt_act, vt_dve = sem("v_hi"), sem("v_lo"), sem("vT_act"), sem("vT_dve")
        router_done, top_zeroed, gap, gap_exp = sem("router_done"), sem("top_zeroed"), sem("gap"), sem("gap_exp")
        sel_ready, pos_done, pos_ready = sem("sel_ready"), sem("pos_done"), sem("pos_ready")
        onehot, ct_done, ct_out = sem("onehot"), sem("combT_done"), sem("combT_out")
        gathered, xg_hi, xg_lo = sem("gathered"), sem("xg_hi"), sem("xg_lo")
        m_silu, m_ff, m_tr, m_thi, m_tlo = (sem("moe_silu"), sem("moe_ff"), sem("moe_ffT"),
                                            sem("moe_ffT_hi"), sem("moe_ffT_lo"))
        m_y, combined, comb_added = sem("moe_y"), sem("combined"), sem("comb_added")
        stored = sem("stored")
        o_landed, o_used, o_onehot, o_gathered, o_ct = (sem("over_landed"), sem("over_used"), sem("over_onehot"),
                                                        sem("over_gathered"), sem("over_combT"))
        o_tokens, o_up, o_silu, o_ff, o_tr = (sem("over_tokens"), sem("over_up"), sem("over_silu"), sem("over_ff"),
                                              sem("over_ffT_psum"))
        over_pos = sem("over_pos")
        o_fft, o_y, o_combined, o_added = (sem("over_ffT"), sem("over_y"),
                                                   sem("over_combined"), sem("over_added"))

        def std(src, c0, n, w):
            return [(src[(c0 + 2 * i) * P:(c0 + 2 * i + 2) * P, :].rearrange("(c p) f -> p c f", p=P), 2 * i, w)
                    for i in range(2)]

        def granule(layer, g):
            if g < G_BR:
                c, w = SLICES[g // 2]
                return std(w_in[layer, :, c:c + w], 4 * (g % 2), 4, w)
            if g < G_OUT:
                n, half = BRANCHES[(g - G_BR) // 2], (g - G_BR) % 2
                return std(w_branch[layer, n, :, half * 512:half * 512 + 512], 0, 4, 512)
            if g < G_FF:
                half, q = (g - G_OUT) // 2, (g - G_OUT) % 2
                return std(w_out[layer, :, half * 512:half * 512 + 512], 4 * q, 4, 512)
            if g >= G_PLE0:
                q = g - G_PLE0
                if q < 4:
                    return std(ple_gate[layer, :, (q // 2) * 512:(q // 2) * 512 + 512], 4 * (q % 2), 4, 512)
                return wide(ple_proj[layer])
            return ff_granule(g - G_FF, lambda a, j, q: a[0, q * 512:(q + 1) * 512, j * FS:(j + 1) * FS],
                              dense_wg, dense_wu, lambda j: dense_wd[0, j * FS:(j + 1) * FS, :])

        def wide(src):
            return [(src[i * P:(i + 1) * P, :], "wide", i) for i in range(2)]

        ORDER = [("up", 0, 0), ("up", 0, 1)]
        for j in range(1, NS):
            ORDER += [("up", j, 0), ("up", j, 1), ("down", j - 1, 0)]
        ORDER += [("down", NS - 1, 0)]

        def ff_granule(k, part, wg, wu, down):
            kind, j, q = ORDER[k]
            if kind == "down":
                return wide(down(j))
            return [(part(a, j, q).rearrange("(c p) f -> p c f", p=P), "gu", i) for i, a in enumerate((wg, wu))]

        def place(slot, how, w):
            r = raw(slot)
            if how == "wide":
                return r[:, w * D:(w + 1) * D]
            if how == "gu":
                return r.rearrange("p (c s f) -> p c s f", c=4, s=2)[:, :, w, :]
            return r.rearrange("p (c f) -> p c f", c=4)[:, how:how + 2, 0:w]

        def slot_cols(n_ring, c, w, c_width=512, off=0):
            a = n_ring * GRAN + c * c_width + off
            return whi[:, a:a + w], wlo[:, a:a + w]

        block = ctx.enter_context(nc.Block())

        AT = {6: [0], 7: [1, 2], 8: [3], 9: [4], 10: [5], 11: [6], 12: [7], 13: [8], 14: [9, 10], 15: [11],
              16: [12], 17: [13], 18: [14], 19: [15], 20: [16], 21: [17, 18], 22: [19]}
        AT.update({g: [g - 3] for g in range(23, 34)})
        N_STEPS = 31
        LEVEL0 = 20
        ACT_STEPS = [0, 4, 5, 6, 7, 8, 9, 10, 14, 15, 16, 17, 18, 19, 29, 30]
        DVE_STEPS = [0, 2, 3, 4, 7, 8, 9, 10, 11, 13, 14, 15, 17, 18, 19] + list(range(20, 31))

        def upto(steps, layer, i):
            return layer * len(steps) + sum(s <= i for s in steps)

        A_BR, A_OUT, A_PLE, NACC = NZ, NZ + 6, NZ + 8, NZ + 10
        ACT_OUT = list(range(NZ)) + [A_PLE, A_PLE + 1]
        DVE_OUT = list(range(9)) + list(range(A_BR, A_PLE))
        QT, KT, K0, K1, BETA, SCAN = T, T + 1024, T + 2048, T + 3072, T + 4096, T + 7168
        SQT, IQT, IKT, CT, KT2, VD = T, T + 1024, T + 1536, T + 1792, T + 2048, T + 2304
        ISC, RELU0, PB, PT0, PT1 = (T + 2560, T + 2688), T + 2944, T + 4096, T + 7168, (T, T + 2944)
        HQ, HK, HF, HS, HACC, HCROSS, HSG, HGS = (T, T + 1024, T + 2048, T + 3072, T + 4096, T + 5120, T + 5632,
                                                  T + 6656)
        HX = (ZHG, ZHG + 1024)
        PNAT = T + 7936
        SA_PARTS = [(8, 128, 0, 0), (4, 256, 1024, 8), (4, 256, 2048, 12)]
        DSIL, DFF = T, T + 512
        LOGITS, COMB, SEL, POS = T, T + 32, T + 64, T + 96
        TOP, GAP = T + 128, T + 160
        VO, FFTO = T + 3072, T + 4096
        SIL, FFN_, CPN, CSB, Y = T + 256, T + 512, T + 768, T + 1024, T + 1536
        VT = T + 3072
        XG, FFT = 2048, 4096

        def blocks(ap, m):
            return ap.rearrange("p (b two m) -> p b two m", two=2, m=m)

        def width_of(n):
            if n >= M0:
                return 512
            g = n % L1
            return SLICES[g // 2][1] if g < G_BR else 512

        def landed_when(n):
            if n < M0:
                return landed[n % RAW], 32 * (n // RAW + 1)
            m = n - M0
            return moe_landed[m % RAW_MOE], 32 * (m // RAW_MOE + 1)

        def raw_of(n):
            return raw(n % RAW) if n < M0 else raw((n - M0) % RAW_MOE)

        def halves(a, ring, w):
            return [a[:, ring * GRAN + 1024 * i:ring * GRAN + 1024 * (i + 1)]
                    .rearrange("p (c f) -> p c f", c=2)[:, :, 0:w] for i in range(2)]

        def head_place(i, heads):
            return (i % 2) * (heads // 2) + (i // 2) % (heads // 2)

        def sa_out(dst, tile, par, first):
            r = slice(DH * par, DH * par + DH)
            a = 1 if tile == 0 else 2
            return (dst[r, 3072:4096].rearrange("p (a c k t) -> p a c k t", a=a, k=2, t=P)[:, :, :, tile, :],
                    bank(first, 1024)[r].rearrange("p (a k c t) -> p a k c t", a=a, k=2, t=P)[:, :, par, :, :])

        N_ALL = M0 + N_MOE + 5

        def in_experts(n):
            return n >= M0

        def overflow(eng):
            eng.wait_ge(pos_ready, 1)
            return eng.If(eng.value_load(biggest[0:1, 0:1]) > P)

        @block.sync
        def _(sp):
            def split(n, it=0):
                value = it * (4 * PER_E) + 2 * (n + 1)
                sp.wait_ge(lo_ready, value)
                sp.wait_ge(lo_pool, value)

            for n in range(M0):
                if n >= RAW:
                    split(n - RAW)
                for src, how, w in granule(n // L1, n % L1):
                    sp.dma_start(place(n % RAW, how, w), src).then_inc(landed[n % RAW], 16)
            split(M0 - 1)
            sp.wait_ge(at_ready, 4 * 6)
            with sp.Fori(0, NE // 2) as it:
                for m in range(2 * PER_E):
                    split(M0 + m - RAW_MOE, it)
                    e = it * 2 + m // PER_E

                    def up(a, j, q):
                        return a[0, bass.ds(e, 1), q * 512:(q + 1) * 512, j * FS:(j + 1) * FS]\
                            .rearrange("e k f -> (e k) f")

                    def down(j):
                        return moe_wd[0, bass.ds(e, 1), j * FS:(j + 1) * FS, :].rearrange("e k f -> (e k) f")

                    for src, how, w in ff_granule(m % PER_E, up, moe_wg, moe_wu, down):
                        sp.dma_start(place(m % RAW_MOE, how, w), src).then_inc(moe_landed[m % RAW_MOE], 16)
            for q in range(5):
                m = N_MOE + q
                split(M0 + m - RAW_MOE)
                for src, how, w in granule(1, G_PLE0 + q):
                    sp.dma_start(place(m % RAW_MOE, how, w), src).then_inc(moe_landed[m % RAW_MOE], 16)
            split(M0 + N_MOE - 1)
            with overflow(sp):
                with sp.Fori(0, NE) as e:
                    with sp.Fori(0, NS) as j:
                        def over_up(a, _, q):
                            return a[0, bass.ds(e, 1), q * 512:(q + 1) * 512, bass.ds(j * FS, FS)]\
                                .rearrange("e k f -> (e k) f")

                        def over_down(_):
                            return moe_wd[0, bass.ds(e, 1), bass.ds(j * FS, FS), :].rearrange("e k f -> (e k) f")

                        for q in range(3):
                            sp.wait_ge(o_used, e * (3 * NS + 1) + j * 3 + q + 1)
                            for src, how, w in ff_granule((0, 1, PER_E - 1)[q], over_up, moe_wg, moe_wu, over_down):
                                sp.dma_start(place(RAW_MOE - 1, how, w), src).then_inc(o_landed, 16)
            for t in range(NT):
                sp.wait_ge(u_ready, NT * 3 * DEPTH + t + 1)
                sp.dma_start(out[0, t * P:(t + 1) * P, :], u_nat(t)).then_inc(stored, 16)
            sp.wait_ge(stored, 16 * NT)

        @block.gpsimd
        def _(pool):
            count = [0]

            def link(ins):
                count[0] += 1
                ins.then_inc(pool_chain, 1)
                pool.wait_ge(pool_chain, count[0])

            link(pool.memset(ident[:, :], 0.0))
            link(pool.memset(later[:, :], 0.0))
            pool.memset(ones[:, :], 1.0).then_inc(pool_consts, 1)
            link(pool.memset(neg_half[:, :], -0.5))
            pool.affine_select(out=ident[:, :], in_=ident[:, :], compare_op=ALU.not_equal, fill=1.0,
                               base=0, pattern=[[-1, P]], channel_multiplier=1).then_inc(pool_consts, 1)
            pool.affine_select(out=later[:, :], in_=later[:, :], compare_op=ALU.is_ge, fill=1.0,
                               base=0, pattern=[[-1, P]], channel_multiplier=1).then_inc(pool_consts, 1)
            pool.iota(slots_iota[:, :], [[1, P]], base=0, channel_multiplier=0,
                      allow_small_or_imprecise_dtypes=True).then_inc(pool_consts, 1)
            pool.wait_ge(pool_consts, 4)
            mf = wk(T, 8 * P)
            link(pool.memset(mf, 0.0))
            link(pool.tensor_copy(mf[:, 0:P], ident[:, :]))
            for i in range(7):
                m = 1 << i
                v = blocks(mf[:, (i + 1) * P:(i + 2) * P], m)[:, :, 1, :]
                link(pool.memset(v, 1.0))
                link(pool.affine_select(out=v, in_=v, compare_op=ALU.is_ge, fill=0.0, base=0,
                                        pattern=[[-2 * m, P // (2 * m)], [0, m]], channel_multiplier=1))
                link(pool.affine_select(out=v, in_=v, compare_op=ALU.is_ge, fill=0.0, base=m - 1,
                                        pattern=[[2 * m, P // (2 * m)], [0, m]], channel_multiplier=-1))
            pool.tensor_copy(masks[:, :], mf).then_inc(pool_consts, 1)

            def inverse_root(src, dst, n, over, ready, value, done):
                pool.wait_ge(ready, value)
                link(pool.tensor_scalar(src, src, 1.0 / over, EPS, ALU.mult, ALU.add))
                pool.tensor_tensor(dst, src, neg_half[:, 0:n], ALU.pow).then_inc(done, 1)

            def norm(r):
                inverse_root(ss, rstd, 2, D, squares, 2 * (r + 1), rstd_ready)

            def split_lo(ring, src, w, chunks):
                o, v, a = (halves(x, y, w)[1][:, 2 - chunks:2, :] for x, y in ((wlo, ring), (src, 0), (whi, ring)))
                pool.tensor_tensor(o, v, a.bitcast(f32), ALU.subtract).then_inc(lo_pool, 2)

            def convert(n):
                if n < N_ALL:
                    pool.wait_ge(hi_ready, 2 * n + 2)
                    split_lo(n % WR, raw_of(n), width_of(n), 1 if in_experts(n) else 2)

            def sb_mask(layer, part):
                keep, beta = wk(K0 if part != 1 else K1, 1024), wk(BETA + 1024 * part, 1024)
                for k, (a, fill) in enumerate(((keep, 1.0), (beta, 0.0))):
                    pool.wait_ge(sb_sig, 2 * (3 * layer + part) + k + 1)
                    v, heads = (a.rearrange("p (h s) -> p h s", h=8), 8) if part == 0 else \
                        (a.rearrange("p (h s) -> p h s", h=4)[:, :, P:2 * P], 4)
                    pool.affine_select(out=v, in_=v, compare_op=ALU.is_gt, fill=fill, base=0,
                                       pattern=[[0, heads], [-1, P]], channel_multiplier=1).then_inc(sb_masked, 1)

            def mixer(layer, i):
                if i in (1, 2, 3):
                    sb_mask(layer, i - 1)
                elif i == 4:
                    inverse_root(css, crstd, 2, P, c_squares, 2 * (layer + 1), c_rstd)
                elif i == 19:
                    hg3 = wk(ZHG + 3 * 1024, 1024).rearrange("p (a v) -> p a v", v=P)
                    pool.wait_ge(hg_gsig, layer + 1)
                    pool.wait_ge(layer_consts, 96 * (layer + 1))
                    link(pool.tensor_tensor(hg3, hg3, wk(HGS, 1024).rearrange("p (a v) -> p a v", v=P), ALU.mult))
                    pool.tensor_tensor(hg3, hg3, onorm[:, :].unsqueeze(1).broadcast_to([P, 8, P]), ALU.mult)\
                        .then_inc(hg_gs, 1)
                elif i == 29:
                    inverse_root(hss, hrstd, 8, P, hg_ss, layer + 1, hg_rstd)

            for n in range(WR):
                convert(n)
            for layer in range(DEPTH):
                base = layer * L1
                norm(3 * layer)
                for g in range(G_FF):
                    for i in AT.get(g, []):
                        mixer(layer, i)
                    convert(base + g + WR)
                norm(3 * layer + 1)
                if layer == 0:
                    for g in range(G_FF, G_PLE0):
                        convert(g + WR)
                else:
                    with pool.Fori(0, NE // 2) as it:
                        for m in range(2 * PER_E):
                            pool.wait_ge(hi_ready, it * (4 * PER_E) + 2 * (M0 + m + WR) + 2)
                            split_lo((M0 + m) % WR, raw((m + WR) % RAW_MOE), 512, 1)
                first = base + G_PLE0 if layer == 0 else M0 + N_MOE
                norm(3 * layer + 2)
                for q in range(5):
                    convert(first + q + WR)
            norm(3 * DEPTH)

        @block.scalar
        def _(act):
            def copy(dst, src):
                return nc.scalar.activation(dst, src, ACT.Copy)

            def split_hi(ring, src, w):
                for o, v in zip(halves(whi, ring, w), halves(src, 0, w)):
                    copy(o, v).then_inc(hi_ready, 1)

            def convert(n):
                if n >= N_ALL:
                    return
                act.wait_ge(*landed_when(n))
                if n >= WR:
                    act.wait_ge(gemm_done, n - WR + 1)
                split_hi(n % WR, raw_of(n), width_of(n))

            def load_gain(r):
                src = (norm_mix, norm_ffn, norm_ple)[r % 3][r // 3] if r < 3 * DEPTH else norm_final
                act.dma_start(gain(r), src.partition_broadcast(P)).then_inc(gain_landed[r % 2], 16)

            def load_layer_consts(layer):
                for dst, src in ((cnorm, sa_cnorm[layer]), (onorm, hg_onorm[layer])):
                    act.dma_start(dst[:, :], src.partition_broadcast(P)).then_inc(layer_consts, 16)
                for dst, src in ((wk2, sa_wk[layer]), (wv2, sa_wv[layer])):
                    for i in range(2):
                        act.dma_start(dst[:, i * DH:(i + 1) * DH], src).then_inc(layer_consts, 16)

            def norm_squares(ready, value):
                act.wait_ge(ready, value)
                for t in range(NT):
                    nc.scalar.activation(u_nat(t), h[:, t * D:(t + 1) * D], ACT.Square,
                                         accum_out=ss[:, t:t + 1]).then_inc(squares, 1)

            transposed = [0]

            def hi_of_transposes():
                for b in range(4):
                    transposed[0] += 1
                    act.wait_ge(at_ready, transposed[0])
                    copy(ahi[:, b * 512:(b + 1) * 512], bank(4 + b)).then_inc(at_hi, 1)

            def sb_sigmoids(part, first):
                keep, beta = wk(K0 if part != 1 else K1, 1024), wk(BETA + 1024 * part, 1024)
                nc.scalar.activation(keep, bank(first, 1024), ACT.Sigmoid, scale=-SCALE).then_inc(sb_sig, 1)
                nc.scalar.activation(beta, bank(first, 1024), ACT.Sigmoid, scale=SCALE).then_inc(sb_sig, 1)

            def exps(layer, part):
                heads, n, off, col = SA_PARTS[part]
                act.wait_ge(sa_neg_max, 3 * layer + part + 1)
                for i in range(heads):
                    v = wk(PB + off + i * n, n)
                    last = nc.scalar.activation(v, v, ACT.Exp, bias=nmx[:, col + i:col + i + 1], scale=SCALE,
                                                accum_out=sums[:, col + i:col + i + 1])
                last.then_inc(sa_exp, 1)

            def mixer(layer, i):
                if i not in (11,) and i < 20 or i >= 29:
                    act.wait_ge(pe_step, layer * N_STEPS + i + 1)
                if i == 0:
                    copy(wk(QT, 1024), bank(4, 1024)).then_inc(act_step, 1)
                elif i in (1, 2, 3):
                    if i == 3:
                        act.wait_ge(dve_step, upto(DVE_STEPS, layer, 2))
                    sb_sigmoids(i - 1, 6 if i == 2 else 4)
                elif i in (4, 5, 6):
                    if i == 4:
                        act.wait_ge(dve_step, upto(DVE_STEPS, layer, 3))
                    copy(wk((K1, QT, KT)[i - 4], 1024), bank((6, 4, 6)[i - 4], 1024)).then_inc(act_step, 1)
                    if i == 4:
                        act.wait_ge(acc_out_act, upto(ACT_OUT, layer, 4))
                        act.wait_ge(acc_out_dve, upto(DVE_OUT, layer, 4))
                        for t in range(NT):
                            nc.scalar.activation(wk(T + 8200, P), zs(4, t)[:, 0:P], ACT.Square,
                                                 accum_out=css[:, t:t + 1]).then_inc(c_squares, 1)
                            act.wait_ge(c_squares, 2 * layer + t + 1)
                elif i == 7:
                    copy(ahi[:, 2048:3072], bank(4, 1024)).then_inc(act_step, 1)
                elif i == 8:
                    copy(wk(SQT, 1024), bank(6, 1024)).then_inc(act_step, 1)
                elif i == 9:
                    nc.scalar.activation(wk(RELU0, 512), bank(7), ACT.Relu).then_inc(sa_relu, 1)
                    copy(wk(KT2, 512), bank(6)).then_inc(act_step, 1)
                elif i == 10:
                    nc.scalar.activation(wk(PB, 1024), bank(4, 1024), ACT.Relu).then_inc(act_step, 1)
                elif i in (12, 13):
                    exps(layer, i - 12)
                elif i in (14, 15, 16):
                    copy(wk((PT0, PT1[0], PT1[1])[i - 14], 1024), bank((4, 6, 4)[i - 14], 1024)).then_inc(act_step, 1)
                    if i == 14:
                        exps(layer, 2)
                elif i in (17, 18):
                    for par in range(2):
                        last = copy(*sa_out(ahi, i - 17, par, 6 if i == 17 else 4))
                    last.then_inc(act_step, 1)
                elif i == 19:
                    nc.scalar.activation(wk(HSG, 1024), bank(6, 1024), ACT.Sigmoid).then_inc(hg_sig, 1)
                    nc.scalar.activation(wk(HF, 1024), bank(4, 1024), ACT.Sigmoid).then_inc(hg_sig, 1)
                    nc.scalar.activation(wk(HK, 1024), bank(4, 1024), ACT.Sigmoid, scale=-1.0).then_inc(act_step, 1)
                    act.wait_ge(acc_out_dve, upto(DVE_OUT, layer, 8))
                    nc.scalar.activation(wk(HGS, 1024), wk(ZHG + 3072, 1024), ACT.Sigmoid).then_inc(hg_gsig, 1)
                elif i == 29:
                    nc.scalar.activation(wk(HSG, 1024), bank(6, 1024), ACT.Square).then_inc(act_step, 1)
                elif i == 30:
                    copy(ahi[:, 4096:5120], bank(4, 1024)).then_inc(act_step, 1)

            def ffT_hi(s):
                o = FFT + 256 * (s % 2)
                nc.scalar.activation(ahi[:, o:o + 256], bank(4, 256), ACT.Copy).then_inc(m_thi, 1)

            for t in range(NT):
                act.dma_start(h[:, t * D:(t + 1) * D], x[0, t * P:(t + 1) * P, :]).then_inc(x_landed, 16)
            load_gain(0)
            for i in range(DEPTH):
                act.dma_start(lbp[:, i * HG_H:(i + 1) * HG_H],
                              lb_param[i].rearrange("(h d) -> d h", d=P), allow_slow_non_contiguous=True).then_inc(consts, 16)
            act.dma_start(router[:, :].rearrange("p (c e) -> p c e", e=NE),
                          moe_router[0].rearrange("(c p) e -> p c e", p=P)).then_inc(consts, 16)
            load_layer_consts(0)
            act.wait_ge(lb_shifted, 1)
            nc.scalar.activation(lbt[:, 0:8], lbt[:, 0:8], ACT.Exp).then_inc(lb_exp, 1)
            for n in range(WR):
                convert(n)

            for layer in range(DEPTH):
                base = layer * L1
                norm_squares(*((x_landed, 32) if layer == 0 else (ple_added, layer)))
                hi_of_transposes()
                for g in range(G_OUT):
                    if g % 2 == 1 and g < G_BR:
                        s = g // 2
                        act.wait_ge(gemm_done, base + g + 1)
                        b = 2 * (s + layer * NACC & 1)
                        if s < 9:
                            copy(zs(s, 0, SLICES[s][1]), bank(b, SLICES[s][1])).then_inc(acc_out_act, 1)
                        else:
                            if s == 9:
                                act.wait_ge(pe_step, layer * N_STEPS + 9)
                                act.wait_ge(dve_step, upto(DVE_STEPS, layer, 10))
                            nc.scalar.activation(zs(s, 0, 1024), bank(b, 1024), ACT.Sigmoid).then_inc(acc_out_act, 1)
                    for i in AT.get(g, []):
                        mixer(layer, i)
                    convert(base + g + WR)
                act.wait_ge(dve_step, upto(DVE_STEPS, layer, 30))
                load_gain(3 * layer + 1)
                load_gain(3 * layer + 2)
                act.dma_start(wk(PNAT, NT * PLE).rearrange("p (t f) -> p t f", t=NT),
                              p[layer, 0].rearrange("(t q) f -> q t f", q=P)).then_inc(p_landed, 16)
                if layer == 0:
                    load_layer_consts(1)
                hi_of_transposes()
                for g in range(G_OUT, G_FF):
                    convert(base + g + WR)
                norm_squares(acc_out_dve, upto(DVE_OUT, layer, A_OUT + 1))
                if layer == 0:
                    hi_of_transposes()
                    for k, (kind, j, q) in enumerate(ORDER):
                        if kind == "up" and q == 1:
                            act.wait_ge(gemm_done, base + G_FF + k + 1)
                            for t in range(NT):
                                nc.scalar.activation(wk(DSIL + t * FS, FS), bank(t, FS), ACT.Silu).then_inc(d_silu, 1)
                            if j == 0:
                                act.wait_ge(d_tr, 1)
                                copy(ahi[:, 2048:2560], bank(6)).then_inc(d_thi, 1)
                        if kind == "down" and j + 1 < NS:
                            act.wait_ge(d_tr, j + 2)
                            i = (j + 1) % 2
                            copy(ahi[:, 2048 + 512 * i:2560 + 512 * i], bank(6 + i)).then_inc(d_thi, 1)
                        convert(base + G_FF + k + WR)
                else:
                    act.wait_ge(u_ready, NT * 5)
                    for t in range(NT):
                        copy(ahi[:, t * D:(t + 1) * D], u_nat(t)).then_inc(v_hi, 1)
                    transposed[0] += 4
                    act.wait_ge(at_ready, transposed[0])
                    copy(wk(VT, 1024), bank(4, 1024)).then_inc(vt_act, 1)
                    act.wait_ge(gap, NT)
                    nc.scalar.activation(wk(GAP, 2), wk(GAP, 2), ACT.Exp).then_inc(gap_exp, 1)

                    def xg_hi_of(q, half, value):
                        act.wait_ge(gathered, value)
                        copy(ahi[:, XG + q * 1024 + half * 512:XG + q * 1024 + half * 512 + 512],
                             bank(6 + half)).then_inc(xg_hi, 1)

                    def comb_out(q, value):
                        act.wait_ge(ct_done, value)
                        copy(wk(CSB + q * 256, 256), bank(5, 256)).then_inc(ct_out, 1)

                    comb_out(0, 1)
                    for half in range(2):
                        xg_hi_of(0, half, half + 1)
                    with act.Fori(0, NE // 2) as it:
                        for q in range(2):
                            for k, (kind, j, part) in enumerate(ORDER):
                                m = q * PER_E + k
                                s = q * NS + j
                                if kind == "up" and part == 0 and j > 0:
                                    act.wait_ge(m_tr, it * (2 * NS) + s)
                                    ffT_hi(s - 1)
                                if kind == "up" and part == 1:
                                    act.wait_ge(gemm_done, it * (2 * PER_E) + M0 + m + 1)
                                    nc.scalar.activation(wk(SIL, FS), bank(s % 2, FS), ACT.Silu).then_inc(m_silu, 1)
                                if k == PER_E - 2:
                                    act.wait_ge(m_tr, it * (2 * NS) + s + 2)
                                    ffT_hi(s + 1)
                                if k == PER_E - 1:
                                    act.wait_ge(gemm_done, it * (2 * PER_E) + M0 + m + 1)
                                    act.wait_ge(combined, it * 4 + 2 * q + 2)
                                    copy(wk(Y, 1024), bank(2, 1024)).then_inc(m_y, 1)
                                act.wait_ge(moe_landed[(m + WR) % RAW_MOE],
                                            it * (32 * 2 * PER_E // RAW_MOE) + 32 * ((m + WR) // RAW_MOE + 1))
                                act.wait_ge(gemm_done, it * (2 * PER_E) + M0 + m + 1)
                                split_hi((M0 + m) % WR, raw((m + WR) % RAW_MOE), 512)
                                if kind == "down" and j == 6:
                                    comb_out(1 - q, it * 2 + q + 2)
                                if kind == "down" and j in (8, 9):
                                    xg_hi_of(1 - q, j - 8, it * 4 + 2 * q + j - 8 + 3)
                    with overflow(act):
                        with act.Fori(0, NE * NS) as u:
                            act.wait_ge(o_up, u + 1)
                            nc.scalar.activation(wk(SIL, FS), bank(0, FS), ACT.Silu).then_inc(o_silu, 1)
                act.wait_ge(pt_ready, layer + 1)
                copy(ahi[:, 4096:4608], bank(0)).then_inc(pt_hi, 1)
                norm_squares(ffn_added, layer + 1)
                hi_of_transposes()
                first = base + G_PLE0 if layer == 0 else M0 + N_MOE
                for q in range(5):
                    if q in (1, 3):
                        a = layer * NACC + A_PLE + q // 2
                        act.wait_ge(gemm_done, first + q + 1)
                        o = wk(T, 2048).rearrange("p (t f) -> p t f", t=NT)[:, :, (q // 2) * 512:(q // 2) * 512 + 512]
                        nc.scalar.activation(o, bank(2 * (a % 2), 1024).rearrange("p (t f) -> p t f", t=NT),
                                             ACT.Sigmoid).then_inc(acc_out_act, 1)
                    convert(first + q + WR)
                load_gain(3 * layer + 3)
            norm_squares(ple_added, DEPTH)

        @block.vector
        def _(dve):
            V = nc.vector
            count = [0]

            def link(ins):
                count[0] += 1
                ins.then_inc(dve_chain, 1)
                dve.wait_ge(dve_chain, count[0])

            def lo_of(dst, src, hi):
                return V.tensor_tensor(dst, src, hi.bitcast(f32), ALU.subtract)

            def split_lo(ring, src, w, wait, chunks=2):
                for i, (o, v, a) in enumerate(zip(halves(wlo, ring, w), halves(src, 0, w), halves(whi, ring, w))):
                    if i == 1 and chunks == 0:
                        break
                    wait(i)
                    if i == 1:
                        o, v, a = (x[:, 0:chunks, :] for x in (o, v, a))
                    lo_of(o, v, a).then_inc(lo_ready, 2 if chunks == 0 else 1)

            def convert(n):
                if n < N_ALL:
                    split_lo(n % WR, raw_of(n), width_of(n), lambda i: dve.wait_ge(hi_ready, 2 * n + i + 1),
                             chunks=1 if in_experts(n) else 0)

            def norm(r):
                dve.wait_ge(rstd_ready, r + 1)
                dve.wait_ge(gain_landed[r % 2], 16 * (r // 2 + 1))
                for t in range(NT):
                    V.scalar_tensor_tensor(out=u_nat(t), in0=h[:, t * D:(t + 1) * D], scalar=rstd[:, t:t + 1],
                                           in1=gain(r), op0=ALU.mult, op1=ALU.mult).then_inc(u_ready, 1)

            split = [0]

            def lo_of_transposes():
                for b in range(4):
                    split[0] += 1
                    dve.wait_ge(at_hi, split[0])
                    lo_of(alo[:, b * 512:(b + 1) * 512], bank(4 + b), ahi[:, b * 512:(b + 1) * 512])\
                        .then_inc(at_lo, 1)

            def sb_scan(layer, part):
                heads, n = ((8, 128), (4, 256), (4, 256))[part]
                keep, beta = wk(K0 if part != 1 else K1, 1024), wk(BETA + 1024 * part, 1024)
                scan = wk(SCAN, heads * (n + 1)).rearrange("p (h s) -> p h s", h=heads)
                dve.wait_ge(sb_masked, 2 * (3 * layer + part + 1))
                if part > 0:
                    dve.wait_ge(dve_step, upto(DVE_STEPS, layer, part + 1))
                V.memset(scan[:, :, n:n + 1], 1.0)
                for i in range(heads):
                    last = V.tensor_tensor_scan(scan[:, i, 0:n][:, ::-1], keep[:, i * n:(i + 1) * n][:, ::-1],
                                                zero[:, 0:1].broadcast_to([P, n]), 1.0, ALU.mult, ALU.add)
                link(last)
                b = beta.rearrange("p (h s) -> p h s", h=heads)
                V.tensor_tensor(b, b, scan[:, :, 1:n + 1], ALU.mult).then_inc(dve_step, 1)

            def index_scores(layer, tile):
                n = P * (tile + 1)
                isc, r = wk(ISC[tile], n), wk(PB if tile else RELU0, 4 * n)
                for i in range(IDX_H):
                    w = iwh[:, 4 * tile + i:4 * tile + i + 1]
                    ri = r[:, head_place(i, IDX_H) * n:(head_place(i, IDX_H) + 1) * n]
                    if i == 0:
                        link(V.tensor_scalar(isc, ri, w, None, ALU.mult))
                    else:
                        link(V.scalar_tensor_tensor(out=isc, in0=ri, scalar=w, in1=isc,
                                                    op0=ALU.mult, op1=ALU.add))
                return V.memset(isc[0:64, n - 64:n], MASKED)

            def select_top(tile):
                isc = wk(ISC[tile], P * (tile + 1))
                for _ in range(TOPK // 8):
                    link(V.max(top8, isc))
                    link(V.match_replace(isc, top8, isc, REPLACED))
                return V.tensor_scalar(isc, isc, REPLACED, MASKED, ALU.not_equal, ALU.mult)

            def sa_logits(layer, part, first):
                heads, n, off, col = SA_PARTS[part]
                pb = wk(PB + off, heads * n).rearrange("p (h s) -> p h s", h=heads)
                bias = wk(ISC[0 if part == 0 else 1], n).unsqueeze(1).broadcast_to([P, heads, n])
                link(V.tensor_tensor(pb, bank(first, 1024).rearrange("p (h s) -> p h s", h=heads), bias, ALU.add))
                link(V.reduce_max(mx[:, col:col + heads], pb, AX.X))
                V.tensor_scalar(nmx[:, col:col + heads], mx[:, col:col + heads], -SCALE, None, ALU.mult)\
                    .then_inc(sa_neg_max, 1)

            def sa_normalise(layer, part):
                heads, n, off, col = SA_PARTS[part]
                dve.wait_ge(sa_exp, 3 * layer + part + 1)
                pb = wk(PB + off, heads * n).rearrange("p (h s) -> p h s", h=heads)
                link(V.reciprocal(rsums[:, col:col + heads], sums[:, col:col + heads]))
                return V.tensor_tensor(pb, pb, rsums[:, col:col + heads].unsqueeze(2).broadcast_to([P, heads, n]),
                                       ALU.mult)

            def hg_grow(m):
                f, s = blocks(wk(HF, 1024), m), blocks(wk(HS, 1024), m)
                n = 512 // m
                link(V.tensor_tensor(s[:, :, 0, :], s[:, :, 0, :],
                                     f[:, :, 1, m - 1:m].broadcast_to([P, n, m]), ALU.mult))
                link(V.tensor_tensor(f[:, :, 1, :], f[:, :, 1, :],
                                     f[:, :, 0, m - 1:m].broadcast_to([P, n, m]), ALU.mult))

            def hg_build(level):
                m = 1 << level
                xs, k, s, q, f = (blocks(wk(o, 1024), m) for o in (HX[level % 2], HK, HS, HQ, HF))
                V.tensor_tensor(xs[:, :, 0, :], k[:, :, 0, :], s[:, :, 0, :], ALU.mult)
                V.tensor_tensor(xs[:, :, 1, :], q[:, :, 1, :], f[:, :, 1, :], ALU.mult).then_inc(hg_x, 1)

            def mixer(layer, i):
                if i in (1, 5, 6, 16):
                    return
                if i not in (2, 3, 4, 15):
                    dve.wait_ge(pe_step, layer * N_STEPS + i + 1)
                if i == 0:
                    V.tensor_copy(wk(KT, 1024), bank(6, 1024)).then_inc(dve_step, 1)
                elif i in (2, 3, 4):
                    sb_scan(layer, i - 2)
                    if i == 4:
                        dve.wait_ge(c_rstd, layer + 1)
                        dve.wait_ge(layer_consts, 96 * (layer + 1))
                        for t in range(NT):
                            c = zs(4, t)[:, 0:P]
                            V.tensor_scalar(iwh[:, 4 * t:4 * t + 4], zs(4, t)[:, 448:452], IDX_H ** -0.5, None, ALU.mult)
                            last = V.scalar_tensor_tensor(out=c, in0=c, scalar=crstd[:, t:t + 1], in1=cnorm[:, :],
                                                          op0=ALU.mult, op1=ALU.mult)
                        last.then_inc(c_ready, 1)
                elif i == 7:
                    dve.wait_ge(act_step, upto(ACT_STEPS, layer, 7))
                    lo_of(alo[:, 2048:3072], bank(4, 1024), ahi[:, 2048:3072]).then_inc(dve_step, 1)
                elif i == 8:
                    V.tensor_copy(wk(IQT, 1024), bank(4, 1024)).then_inc(dve_step, 1)
                elif i == 9:
                    dve.wait_ge(sa_relu, layer + 1)
                    dve.wait_ge(c_ready, layer + 1)
                    index_scores(layer, 0).then_inc(dve_step, 1)
                elif i == 10:
                    dve.wait_ge(act_step, upto(ACT_STEPS, layer, 10))
                    link(index_scores(layer, 1))
                    select_top(0).then_inc(dve_step, 1)
                elif i == 11:
                    select_top(1).then_inc(dve_step, 1)
                    dve.wait_ge(dve_step, upto(DVE_STEPS, layer, 11))
                elif i == 12:
                    sa_logits(layer, 0, 6)
                elif i == 13:
                    sa_logits(layer, 1, 4)
                    sa_normalise(layer, 0).then_inc(dve_step, 1)
                elif i == 14:
                    sa_logits(layer, 2, 6)
                    sa_normalise(layer, 1).then_inc(dve_step, 1)
                elif i == 15:
                    sa_normalise(layer, 2).then_inc(dve_step, 1)
                elif i in (17, 18):
                    dve.wait_ge(act_step, upto(ACT_STEPS, layer, i))
                    for par in range(2):
                        o, s = sa_out(alo, i - 17, par, 6 if i == 17 else 4)
                        last = lo_of(o, s, sa_out(ahi, i - 17, par, 6)[0])
                    last.then_inc(dve_step, 1)
                elif i == 19:
                    V.memset(wk(HS, 1024), 1.0)
                    V.memset(wk(HACC, 1024), 0.0)
                    dve.wait_ge(hg_sig, 2 * layer + 1)
                    V.tensor_tensor(wk(HQ, 1024), bank(6, 1024), wk(HSG, 1024), ALU.mult)
                    dve.wait_ge(hg_sig, 2 * layer + 2)
                    dve.wait_ge(act_step, upto(ACT_STEPS, layer, 19))
                    dve.wait_ge(lb_done, 1)
                    for hh in range(HG_H):
                        f, k = wk(HF + hh * SEQ, SEQ), wk(HK + hh * SEQ, SEQ)
                        j = layer * HG_H + hh
                        V.tensor_scalar(k, k, oml[:, j:j + 1], None, ALU.mult)
                        last = V.tensor_scalar(f, f, oml[:, j:j + 1], lb[:, j:j + 1], ALU.mult, ALU.add)
                    last.then_inc(dve_step, 1)
                    dve.wait_ge(dve_step, upto(DVE_STEPS, layer, 19))
                elif i < 28:
                    level = i - LEVEL0
                    if level > 0:
                        hg_grow(1 << (level - 1))
                    hg_build(level)
                    acc = wk(HACC, 1024).rearrange("p (a t) -> p a t", t=P)
                    V.copy_predicated(acc, masks[:, level * P:(level + 1) * P].unsqueeze(1).broadcast_to([P, 8, P]),
                                      bank(4 if level % 2 == 0 else 6, 1024).rearrange("p (a t) -> p a t", t=P))\
                        .then_inc(dve_step, 1)
                    dve.wait_ge(dve_step, upto(DVE_STEPS, layer, i))
                elif i == 28:
                    V.tensor_copy(wk(HCROSS, 512), bank(4)).then_inc(dve_step, 1)
                elif i == 29:
                    dve.wait_ge(act_step, upto(ACT_STEPS, layer, 29))
                    V.reduce_sum(hss, wk(HSG, 1024).rearrange("p (a v) -> p a v", v=P), AX.X).then_inc(hg_ss, 1)
                    dve.wait_ge(hg_rstd, layer + 1)
                    dve.wait_ge(hg_gs, layer + 1)
                    o = wk(HGS, 1024).rearrange("p (a v) -> p a v", v=P)
                    link(V.tensor_tensor(o, bank(6, 1024).rearrange("p (a v) -> p a v", v=P),
                                         hrstd.unsqueeze(2).broadcast_to([P, 8, P]), ALU.mult))
                    V.tensor_tensor(wk(HGS, 1024), wk(HGS, 1024), wk(ZHG + 3072, 1024), ALU.mult).then_inc(dve_step, 1)
                elif i == 30:
                    dve.wait_ge(act_step, upto(ACT_STEPS, layer, 30))
                    lo_of(alo[:, 4096:5120], bank(4, 1024), ahi[:, 4096:5120]).then_inc(dve_step, 1)

            def add_to_h(out_view, psum_view):
                return V.tensor_tensor(out_view, out_view, psum_view, ALU.add)

            def h_half(half):
                return h[:, :].rearrange("p (t f) -> p t f", t=NT)[:, :, half * 512:half * 512 + 512]

            V.memset(zero[:, :], 0.0)
            dve.wait_ge(consts, 48)
            l0, l1 = lbp[:, 0:HG_H], lbp[:, HG_H:2 * HG_H]
            link(V.tensor_tensor(lbt[:, 8:12], l0, l1, ALU.max))
            V.tensor_tensor(lbt[:, 0:4], l0, lbt[:, 8:12], ALU.subtract)
            V.tensor_tensor(lbt[:, 4:8], l1, lbt[:, 8:12], ALU.subtract).then_inc(lb_shifted, 1)
            dve.wait_ge(lb_exp, 1)
            link(V.tensor_tensor(lbt[:, 8:12], lbt[:, 0:4], lbt[:, 4:8], ALU.add))
            link(V.reciprocal(lbt[:, 12:16], lbt[:, 8:12]))
            V.tensor_tensor(lbt[:, 0:4], lbt[:, 0:4], lbt[:, 12:16], ALU.mult)
            link(V.tensor_tensor(lbt[:, 4:8], lbt[:, 4:8], lbt[:, 12:16], ALU.mult))
            V.tensor_tensor(lb[:, 0:4], lbt[:, 0:4], lbt[:, 0:4], ALU.subtract)
            link(V.tensor_tensor(lb[:, 4:8], lbt[:, 0:4], lbt[:, 4:8], ALU.add))
            link(V.tensor_tensor(lb[:, 4:8], lb[:, 4:8], lbt[:, 0:4], ALU.subtract))
            V.tensor_scalar(oml[:, :], lb[:, :], -1.0, 1.0, ALU.mult, ALU.add).then_inc(lb_done, 1)
            dve.wait_ge(pool_consts, 5)
            for n in range(WR):
                convert(n)

            for layer in range(DEPTH):
                base = layer * L1
                norm(3 * layer)
                lo_of_transposes()
                for g in range(G_OUT):
                    if g % 2 == 1 and g < 18:
                        s = g // 2
                        dve.wait_ge(gemm_done, base + g + 1)
                        b = 2 * (s + layer * NACC & 1) + 1
                        V.tensor_copy(zs(s, 1, SLICES[s][1]), bank(b, SLICES[s][1])).then_inc(acc_out_dve, 1)
                    if g >= G_BR:
                        bi, half = (g - G_BR) // 2, (g - G_BR) % 2
                        a = layer * NACC + A_BR + g - G_BR
                        dve.wait_ge(gemm_done, base + g + 1)
                        dve.wait_ge(acc_out_act, upto(ACT_OUT, layer, NZ - 1))
                        gt = zs(9 + 2 * bi + half, 0, 1024)
                        ins = V.tensor_tensor(gt, gt, bank(2 * (a % 2), 1024), ALU.mult)
                        ins.then_inc(acc_out_dve, 1)
                        if bi > 0:
                            dve.wait_ge(acc_out_dve, upto(DVE_OUT, layer, A_BR + g - G_BR))
                            m = zs(9 + half, 0, 1024)
                            add = V.tensor_tensor(m, m, gt, ALU.add)
                            if bi == 2:
                                add.then_inc(merged_ready, 1)
                            else:
                                link(add)
                    for i in AT.get(g, []):
                        mixer(layer, i)
                    convert(base + g + WR)
                lo_of_transposes()
                for g in range(G_OUT, G_FF):
                    if (g - G_OUT) % 2 == 1:
                        a = layer * NACC + A_OUT + (g - G_OUT) // 2
                        dve.wait_ge(gemm_done, base + g + 1)
                        add_to_h(h_half((g - G_OUT) // 2),
                                 bank(2 * (a % 2), 1024).rearrange("p (t f) -> p t f", t=NT)).then_inc(acc_out_dve, 1)
                    convert(base + g + WR)
                norm(3 * layer + 1)
                if layer == 0:
                    lo_of_transposes()
                    def ffT_lo(j):
                        dve.wait_ge(d_thi, j + 1)
                        o = slice(2048 + 512 * (j % 2), 2560 + 512 * (j % 2))
                        lo_of(alo[:, o], bank(6 + j % 2), ahi[:, o]).then_inc(d_tlo, 1)

                    for k, (kind, j, q) in enumerate(ORDER):
                        if kind == "up" and q == 1:
                            for t in range(NT):
                                dve.wait_ge(d_silu, 2 * j + t + 1)
                                V.tensor_tensor(wk(DFF + t * FS, FS), wk(DSIL + t * FS, FS), bank(t, FS, FS),
                                                ALU.mult).then_inc(d_ff, 1)
                            if j == 0:
                                ffT_lo(0)
                        if kind == "down" and j + 1 < NS:
                            ffT_lo(j + 1)
                        convert(base + G_FF + k + WR)
                    dve.wait_ge(gemm_done, base + G_PLE0)
                    add_to_h(h[:, :], bank(2, 2048)).then_inc(ffn_added, 1)
                else:
                    for t in range(NT):
                        dve.wait_ge(v_hi, t + 1)
                        lo_of(alo[:, t * D:(t + 1) * D], u_nat(t), ahi[:, t * D:(t + 1) * D]).then_inc(v_lo, 1)
                    dve.wait_ge(at_ready, 4 * 7)
                    V.tensor_copy(wk(VT + 1024, 1024), bank(6, 1024)).then_inc(vt_dve, 1)
                    V.memset(wk(LOGITS, 128), 0.0).then_inc(top_zeroed, 1)
                    dve.wait_ge(top_zeroed, 1)
                    dve.wait_ge(router_done, 1)
                    link(V.tensor_copy(wk(LOGITS, 16), bank(0, 16)))
                    for t in range(NT):
                        lg = wk(LOGITS + 8 * t, 8)
                        link(V.max(wk(TOP + 8 * t, 8), lg))
                        link(V.max_index(wk(TOP + 16 + 8 * t, 8).bitcast(u32), wk(TOP + 8 * t, 8), lg))
                        V.tensor_tensor(wk(GAP + t, 1), wk(TOP + 8 * t + 1, 1), wk(TOP + 8 * t, 1), ALU.subtract)
                        V.tensor_copy(wk(GAP + 4 + 2 * t, 2), wk(TOP + 16 + 8 * t, 2).bitcast(u32)).then_inc(gap, 1)
                    dve.wait_ge(gap_exp, 1)
                    link(V.tensor_scalar(wk(GAP + 8, 2), wk(GAP, 2), 1.0, None, ALU.add))
                    link(V.reciprocal(wk(GAP + 10, 2), wk(GAP + 8, 2)))
                    link(V.tensor_tensor(wk(GAP + 12, 2), wk(GAP + 10, 2), wk(GAP, 2), ALU.mult))
                    for t in range(NT):
                        e8 = slots_iota[:, 0:NE]
                        one, two = wk(GAP + 16, 8), wk(GAP + 24, 8)
                        link(V.tensor_scalar(one, e8, wk(GAP + 4 + 2 * t, 1), None, ALU.is_equal))
                        link(V.tensor_scalar(two, e8, wk(GAP + 5 + 2 * t, 1), None, ALU.is_equal))
                        link(V.tensor_tensor(wk(SEL + 16 * t, 8), one, two, ALU.add))
                        link(V.tensor_scalar(one, one, wk(GAP + 10 + t, 1), None, ALU.mult))
                        V.scalar_tensor_tensor(out=wk(COMB + 16 * t, 8), in0=two, scalar=wk(GAP + 12 + t, 1),
                                               in1=one, op0=ALU.mult, op1=ALU.add).then_inc(sel_ready, 1)
                        dve.wait_ge(sel_ready, t + 1)
                    dve.wait_ge(pos_done, 1)
                    for t in range(NT):
                        V.tensor_copy(wk(POS + 16 * t, 8), bank(1, 8, 8 * t))
                    link(V.reduce_max(wk(GAP + 32, 1), bank(1, 8, 16), AX.X))
                    V.tensor_copy(biggest[:, :], wk(GAP + 32, 1)).then_inc(pos_ready, 1)
                    V.memset(wk(CSB + 256, 256), 0.0)
                    V.memset(wk(Y, 1024), 0.0).then_inc(m_y, 1)
                    dve.wait_ge(pos_ready, 1)

                    def place_tokens(e, done):
                        for t in range(NT):
                            V.tensor_scalar(psel[:, t * P:(t + 1) * P], slots_iota[:, :], col(POS + 16 * t, e),
                                            col(SEL + 16 * t, e), ALU.is_equal, ALU.mult).then_inc(done, 1)
                            V.tensor_scalar(wk(CPN + t * P, P), slots_iota[:, :], col(POS + 16 * t, e),
                                            col(COMB + 16 * t, e), ALU.is_equal, ALU.mult).then_inc(done, 1)

                    def col(first, e):
                        return arena[:, bass.ds(e + first, 1)] if not isinstance(e, int) else wk(first + e, 1)

                    def xg_lo_of(q, half, value):
                        dve.wait_ge(xg_hi, value)
                        o = slice(XG + q * 1024 + half * 512, XG + q * 1024 + half * 512 + 512)
                        lo_of(alo[:, o], bank(6 + half), ahi[:, o]).then_inc(xg_lo, 1)

                    def ffT_lo(s, value):
                        dve.wait_ge(m_thi, value)
                        o = slice(FFT + 256 * (s % 2), FFT + 256 * (s % 2) + 256)
                        lo_of(alo[:, o], bank(4, 256), ahi[:, o]).then_inc(m_tlo, 1)

                    def add_combined(t, value):
                        dve.wait_ge(combined, value)
                        add_to_h(h[:, t * D:(t + 1) * D], bank(6, 1024)).then_inc(comb_added, 1)

                    place_tokens(0, onehot)
                    for half in range(2):
                        xg_lo_of(0, half, half + 1)
                    with dve.Fori(0, NE // 2) as it:
                        for q in range(2):
                            for k, (kind, j, part) in enumerate(ORDER):
                                m = q * PER_E + k
                                s = q * NS + j
                                if kind == "up" and part == 0 and j > 0:
                                    ffT_lo(s - 1, it * (2 * NS) + s)
                                if kind == "up" and part == 1:
                                    dve.wait_ge(m_silu, it * (2 * NS) + s + 1)
                                    V.tensor_tensor(wk(FFN_, FS), wk(SIL, FS), bank(s % 2, FS, FS), ALU.mult)\
                                        .then_inc(m_ff, 1)
                                if k == PER_E - 2:
                                    ffT_lo(s + 1, it * (2 * NS) + s + 2)
                                split_lo((M0 + m) % WR, raw((m + WR) % RAW_MOE), 512,
                                         lambda i: dve.wait_ge(hi_ready, it * (4 * PER_E) + 2 * (M0 + m + WR) + i + 1),
                                         chunks=1)
                                if kind == "down" and j == 1:
                                    dve.wait_ge(gathered, it * 4 + 2 * q + 2)
                                    dve.wait_ge(ct_done, it * 2 + q + 1)
                                    place_tokens(it * 2 + (q + 1), onehot)
                                if kind == "down" and j in (2, 4):
                                    t = (j - 2) // 2
                                    add_combined(t, it * 4 + 2 * q + t + 1)
                                if kind == "down" and j in (8, 9):
                                    xg_lo_of(1 - q, j - 8, it * 4 + 2 * q + j - 8 + 3)
                    for t in range(NT):
                        add_combined(t, 2 * NE + t + 1)
                        dve.wait_ge(comb_added, 2 * NE + t + 1)
                    with overflow(dve):
                        for t in range(NT):
                            last = V.tensor_scalar(wk(POS + 16 * t, NE), wk(POS + 16 * t, NE), -float(P), None, ALU.add)
                        last.then_inc(over_pos, 1)
                        dve.wait_ge(over_pos, 1)
                        with dve.Fori(0, NE) as e:
                            place_tokens(e, o_onehot)
                            V.memset(wk(Y, 1024), 0.0)
                            dve.wait_ge(o_ct, e + 1)
                            V.tensor_copy(wk(CSB, 256), bank(5, 256)).then_inc(o_tokens, 1)
                            dve.wait_ge(o_gathered, e * 2 + 2)
                            V.tensor_copy(wk(VO, 1024), bank(6, 1024)).then_inc(o_tokens, 1)
                            with dve.Fori(0, NS) as j:
                                dve.wait_ge(o_silu, e * NS + j + 1)
                                V.tensor_tensor(wk(FFN_, FS), wk(SIL, FS), bank(0, FS, FS), ALU.mult).then_inc(o_ff, 1)
                                dve.wait_ge(o_tr, e * NS + j + 1)
                                V.tensor_copy(wk(FFTO, 256), bank(4, 256)).then_inc(o_fft, 1)
                                dve.wait_ge(o_used, e * (3 * NS + 1) + j * 3 + 4)
                                V.tensor_tensor(wk(Y, 1024), wk(Y, 1024), bank(2, 1024), ALU.add).then_inc(o_y, 1)
                                dve.wait_ge(o_y, e * NS + j + 1)
                            for t in range(NT):
                                dve.wait_ge(o_combined, e * 2 + t + 1)
                                add_to_h(h[:, t * D:(t + 1) * D], bank(6, 1024)).then_inc(o_added, 1)
                            dve.wait_ge(o_added, e * 2 + 2)
                    V.memset(wk(GAP, 1), 0.0).then_inc(ffn_added, 1)
                dve.wait_ge(pt_hi, layer + 1)
                lo_of(alo[:, 4096:4608], bank(0), ahi[:, 4096:4608]).then_inc(pt_lo, 1)
                norm(3 * layer + 2)
                lo_of_transposes()
                first = base + G_PLE0 if layer == 0 else M0 + N_MOE
                for q in range(5):
                    convert(first + q + WR)
                dve.wait_ge(gemm_done, first + 5)
                dve.wait_ge(acc_out_act, upto(ACT_OUT, layer, A_PLE + 1))
                link(V.tensor_tensor(wk(T, 2048), wk(T, 2048), bank(4, 2048), ALU.mult))
                V.tensor_tensor(h[:, :], h[:, :], wk(T, 2048), ALU.add).then_inc(ple_added, 1)
            norm(3 * DEPTH)


        @block.tensor
        def _(pe):
            TE = nc.tensor

            def three(o, a_col, w_off, n, start, stop):
                sa, sw = slice(a_col, a_col + P), slice(w_off, w_off + n)
                TE.matmul(o, ahi[:, sa], whi[:, sw], start=start, stop=False)
                TE.matmul(o, alo[:, sa], whi[:, sw], start=False, stop=False)
                return TE.matmul(o, ahi[:, sa], wlo[:, sw], start=False, stop=stop)

            def split_ready(n, half):
                if isinstance(n, tuple):
                    pe.wait_ge(lo_ready, n[0] * (4 * PER_E) + 2 * n[1] + half + 1)
                    if half == 1:
                        pe.wait_ge(lo_pool, n[0] * (4 * PER_E) + 2 * n[1] + 2)
                else:
                    pe.wait_ge(lo_ready, 2 * n + half + 1)
                    if half == 1:
                        pe.wait_ge(lo_pool, 2 * n + 2)

            def narrow(n, ring, a_base, chunk, outs, w, a_pitch=SEQ, first=False, last=False):
                for half in range(2):
                    split_ready(n, half)
                    for c in (2 * half, 2 * half + 1):
                        for t, o in enumerate(outs):
                            ins = three(o, a_base + (chunk + c) * a_pitch + t * P, ring * GRAN + c * 512, w,
                                        first and c == 0, last and c == 3)
                ins.then_inc(gemm_done, 1)
                return ins

            def wide_granule(n, ring, a_base, outs, a_pitch, first, last, between=None):
                for c in range(2):
                    if c == 1 and between is not None:
                        between()
                    split_ready(n, c)
                    for t, pair in enumerate(outs):
                        for half, o in enumerate(pair):
                            ins = three(o, a_base + c * a_pitch + t * P, ring * GRAN + c * D + half * 512, 512,
                                        first and c == 0, last and c == 1)
                ins.then_inc(gemm_done, 1)

            splits = [0]

            def wait_at():
                splits[0] += 4
                pe.wait_ge(at_hi, splits[0])
                pe.wait_ge(at_lo, splits[0])

            def transpose_all(src):
                for b in range(4):
                    for c in (2 * b, 2 * b + 1):
                        for t in range(NT):
                            last = TE.transpose(bank(4 + b, P, (c % 2) * SEQ + t * P), src(c, t), ident[:, :])
                    last.then_inc(at_ready, 1)

            def transpose_u(r):
                pe.wait_ge(u_ready, NT * (r + 1))
                transpose_all(lambda c, t: u_nat(t)[:, c * P:(c + 1) * P])

            def acc_free(layer, k):
                if k >= 2:
                    pe.wait_ge(acc_out_act, upto(ACT_OUT, layer, k - 2))
                    if upto(DVE_OUT, layer, k - 2):
                        pe.wait_ge(acc_out_dve, upto(DVE_OUT, layer, k - 2))

            def accs(layer, k, w):
                a = layer * NACC + k
                return [bank(2 * (a % 2) + t, w) for t in range(NT)]

            evens = [0]

            def head_rows(i):
                return slice(DH * (i % 2), DH * (i % 2) + DH)

            def after_act(layer, i):
                pe.wait_ge(act_step, upto(ACT_STEPS, layer, i))

            def after_dve(layer, i):
                pe.wait_ge(dve_step, upto(DVE_STEPS, layer, i))

            def rows_products(q_off, k_off, heads, tile, first, one_bank=False):
                n = P * (tile + 1)
                for k, i in sorted((head_place(i, len(heads)), i) for i in heads):
                    r = head_rows(i)
                    q = q_off + (i // 2) * SEQ + tile * P
                    ko = k_off(i)
                    last = TE.matmul(bank(first, n, k * n), arena[r, q:q + P], arena[r, ko:ko + n],
                                     start=True, stop=True)
                    if one_bank and k == len(heads) // 2 - 1:
                        evens[0] += 1
                        last.then_inc(even_heads, 1)
                        pe.wait_ge(even_heads, evens[0])
                return last

            def transpose_blocks(src, n, first):
                for k in range(n):
                    last = TE.transpose(bank(first, P, k * P), wk(src + k * P, P), ident[:, :])
                return last

            def mixer(layer, i):
                if i == 0:
                    pe.wait_ge(acc_out_act, upto(ACT_OUT, layer, 1))
                    pe.wait_ge(acc_out_dve, upto(DVE_OUT, layer, 1))
                    for s in range(2):
                        for c in range(4):
                            for t in range(NT):
                                last = TE.transpose(bank(4 + 2 * s, P, c * SEQ + t * P),
                                                    zs(s, t)[:, c * P:(c + 1) * P], ident[:, :])
                elif i in (1, 2, 3):
                    after_act(layer, 0)
                    after_dve(layer, 0)
                    if i == 3:
                        pe.wait_ge(sb_sig, 2 * (3 * layer + 1))
                    heads = (range(8), range(4), range(4, 8))[i - 1]
                    last = rows_products(QT, lambda n: KT + (n // 2) * SEQ, heads, 0 if i == 1 else 1, 6 if i == 2 else 4)
                elif i in (4, 5, 6):
                    if i == 6:
                        after_act(layer, 4)
                    else:
                        pe.wait_ge(sb_sig, 2 * (3 * layer + i - 2))
                    after_dve(layer, i - 2)
                    last = transpose_blocks(BETA + 1024 * (i - 4), 8, (6, 4, 6)[i - 4])
                elif i == 7:
                    after_act(layer, 6)
                    pe.wait_ge(acc_out_act, upto(ACT_OUT, layer, 2))
                    pe.wait_ge(acc_out_dve, upto(DVE_OUT, layer, 2))
                    for n in range(SB_H):
                        o = bank(4, SEQ, (n // 2) * SEQ)[head_rows(n)]
                        v = [zs(2, t)[:, n * DH:(n + 1) * DH] for t in range(NT)]
                        TE.matmul(o[:, 0:P], v[0], wk(K1 + head_place(n, 8) * P, P), start=True, stop=True)
                        at1 = (QT if n < 4 else KT) + head_place(n, 4) * SEQ
                        TE.matmul(o[:, P:SEQ], v[0], wk(at1, P), start=True, stop=False)
                        last = TE.matmul(o[:, P:SEQ], v[1], wk(at1 + P, P), start=False, stop=True)
                elif i == 8:
                    after_act(layer, 7)
                    after_dve(layer, 7)
                    pe.wait_ge(c_ready, layer + 1)
                    pe.wait_ge(acc_out_act, upto(ACT_OUT, layer, 4))
                    pe.wait_ge(acc_out_dve, upto(DVE_OUT, layer, 4))
                    for t in range(NT):
                        for c in range(4):
                            TE.transpose(bank(6, P, c * SEQ + t * P), zs(3, t)[:, c * P:(c + 1) * P], ident[:, :])
                        for c in range(2):
                            TE.transpose(bank(4, P, c * SEQ + t * P), zs(4, t)[:, P * (c + 1):P * (c + 2)], ident[:, :])
                        for r in range(2):
                            TE.matmul(bank(5, P, t * P)[head_rows(r)], zs(4, t)[:, 384:448], ident[:, :],
                                      start=True, stop=True)
                        last = TE.transpose(bank(5, P, SEQ + t * P), zs(4, t)[:, 0:P], ident[:, :])
                elif i == 9:
                    after_act(layer, 8)
                    after_dve(layer, 8)
                    pe.wait_ge(layer_consts, 96 * (layer + 1))
                    TE.matmul(bank(6, SEQ), wk2[:, :], wk(CT, SEQ), start=True, stop=True)
                    for t in range(NT):
                        TE.matmul(bank(6, P, SEQ + t * P), wk(CT + t * P, P), wv2[:, :], start=True, stop=True)
                    last = rows_products(IQT, lambda n: IKT, range(4), 0, 7, one_bank=True)
                elif i == 10:
                    last = rows_products(IQT, lambda n: IKT, range(4), 1, 4)
                elif i == 11:
                    after_act(layer, 9)
                    last = rows_products(SQT, lambda n: KT2, range(8), 0, 6)
                elif i == 12:
                    after_act(layer, 10)
                    last = rows_products(SQT, lambda n: KT2, range(4), 1, 4)
                elif i == 13:
                    pe.wait_ge(sa_neg_max, 3 * layer + 1)
                    last = rows_products(SQT, lambda n: KT2, range(4, 8), 1, 6)
                elif i in (14, 15, 16):
                    after_dve(layer, i - 1)
                    if i == 16:
                        after_act(layer, 14)
                    last = transpose_blocks(PB + 1024 * (i - 14), 8, (4, 6, 4)[i - 14])
                elif i == 17:
                    after_act(layer, 15)
                    for half in range(2):
                        last = TE.matmul(bank(6 + half), wk(VD, P), wk(PT0 + half * 512, 512), start=True, stop=True)
                elif i == 18:
                    after_act(layer, 16)
                    for half in range(2):
                        for st in range(NT):
                            pt = wk(PT1[half], 1024).rearrange("p (h k t) -> p h k t", k=2, t=P)[:, :, st, :]
                            last = TE.matmul(bank(4 + half), wk(VD + st * P, P), pt, start=st == 0, stop=st == 1)
                elif i == 19:
                    after_act(layer, 18)
                    after_dve(layer, 18)
                    pe.wait_ge(acc_out_act, upto(ACT_OUT, layer, 6))
                    pe.wait_ge(acc_out_dve, upto(DVE_OUT, layer, 6))
                    for s, first in ((5, 6), (6, 4)):
                        for c in range(HG_H):
                            for t in range(NT):
                                last = TE.transpose(bank(first, P, c * SEQ + t * P),
                                                    zs(s, t)[:, c * P:(c + 1) * P], ident[:, :])
                elif i == 20:
                    after_dve(layer, 19)
                    for k in range(8):
                        last = TE.matmul(bank(4, P, k * P), wk(HK + k * P, P), wk(HQ + k * P, P), start=True, stop=True)
                elif i < 28:
                    level = i - 21
                    pe.wait_ge(hg_x, 8 * layer + level + 1)
                    after_dve(layer, i - 2)
                    for k in range(8):
                        xs = wk(HX[level % 2] + k * P, P)
                        last = TE.matmul(bank(6 if level % 2 == 0 else 4, P, k * P), xs, xs, start=True, stop=True)
                elif i == 28:
                    pe.wait_ge(hg_x, 8 * layer + 8)
                    after_dve(layer, 26)
                    for k in range(HG_H):
                        xs = HX[1] + k * SEQ
                        last = TE.matmul(bank(4, P, k * P), wk(xs, P), wk(xs + P, P), start=True, stop=True)
                elif i == 29:
                    after_dve(layer, 28)
                    for k in range(HG_H):
                        v = [zs(7, t)[:, k * P:(k + 1) * P] for t in range(NT)]
                        TE.matmul(bank(6, P, k * P), wk(HACC + 2 * k * P, P), v[0], start=True, stop=True)
                        TE.matmul(bank(7, P, k * P), wk(HCROSS + k * P, P), v[0], start=True, stop=False)
                        last = TE.matmul(bank(7, P, k * P), wk(HACC + (2 * k + 1) * P, P), v[1], start=False, stop=True)
                elif i == 30:
                    after_dve(layer, 29)
                    for k in range(HG_H):
                        for t in range(NT):
                            last = TE.transpose(bank(4, P, k * SEQ + t * P), wk(HGS + t * 512 + k * P, P), ident[:, :])
                last.then_inc(pe_step, 1)

            pe.wait_ge(pool_consts, 5)
            for layer in range(DEPTH):
                base = layer * L1
                transpose_u(3 * layer)
                wait_at()
                for g in range(G_OUT):
                    n = base + g
                    if g < G_BR:
                        s, q = g // 2, g % 2
                        if q == 0:
                            acc_free(layer, s)
                        narrow(n, n % WR, 0, 4 * q, accs(layer, s, SLICES[s][1]), SLICES[s][1],
                               first=q == 0, last=q == 1)
                    else:
                        k = g - G_BR
                        if k % 2 == 0:
                            after_act(layer, (7, 18, 30)[k // 2])
                            after_dve(layer, (7, 18, 30)[k // 2])
                        acc_free(layer, A_BR + k)
                        narrow(n, n % WR, 2048 + 1024 * (k // 2), 0, accs(layer, A_BR + k, 512), 512,
                               first=True, last=True)
                    for i in AT.get(g, []):
                        mixer(layer, i)
                pe.wait_ge(merged_ready, 2 * (layer + 1))
                transpose_all(lambda c, t: zs(9 + c // 4, t)[:, (c % 4) * P:(c % 4 + 1) * P])
                wait_at()
                for g in range(G_OUT, G_FF):
                    n, half, q = base + g, (g - G_OUT) // 2, (g - G_OUT) % 2
                    if q == 0:
                        acc_free(layer, A_OUT + half)
                    narrow(n, n % WR, 0, 4 * q, accs(layer, A_OUT + half, 512), 512, first=q == 0, last=q == 1)
                transpose_u(3 * layer + 1)
                if layer == 0:
                    wait_at()
                    for k, (kind, j, q) in enumerate(ORDER):
                        n = base + G_FF + k
                        if kind == "up":
                            if q == 0 and j > 0:
                                pe.wait_ge(d_ff, 2 * j)
                            narrow(n, n % WR, 0, 4 * q, [bank(0), bank(1)], 512, first=q == 0, last=q == 1)
                        else:
                            pe.wait_ge(d_thi, j + 1)
                            pe.wait_ge(d_tlo, j + 1)
                            wide_granule(n, n % WR, 2048 + 512 * (j % 2), [(bank(2), bank(3)), (bank(4), bank(5))],
                                         SEQ, j == 0, j == NS - 1)
                        i = 0 if (kind == "up" and q == 1 and j == 0) else j + 1 if kind == "down" else NS
                        if i < NS:
                            pe.wait_ge(d_ff, 2 * i + 2)
                            if i >= 2:
                                pe.wait_ge(d_tlo, i - 1)
                            for c in range(2):
                                for t in range(NT):
                                    last = TE.transpose(bank(6 + i % 2, P, c * SEQ + t * P),
                                                        wk(DFF + t * FS + c * P, P), ident[:, :])
                            last.then_inc(d_tr, 1)
                else:
                    pe.wait_ge(vt_act, 1)
                    pe.wait_ge(vt_dve, 1)
                    pe.wait_ge(consts, 48)
                    for t in range(NT):
                        for c in range(KC):
                            last = TE.matmul(bank(0, NE, NE * t), wk(VT + c * SEQ + t * P, P),
                                             router[:, c * NE:(c + 1) * NE], start=c == 0, stop=c == KC - 1)
                    last.then_inc(router_done, 1)
                    pe.wait_ge(sel_ready, NT)
                    s0, s1 = wk(SEL, NE), wk(SEL + 16, NE)
                    TE.matmul(bank(1, NE, 0), later[:, :], s0, start=True, stop=True)
                    TE.matmul(bank(1, NE, 8), ones[:, :], s0, start=True, stop=False)
                    TE.matmul(bank(1, NE, 8), later[:, :], s1, start=False, stop=True)
                    TE.matmul(bank(1, NE, 16), ones[:, :], s0, start=True, stop=False)
                    TE.matmul(bank(1, NE, 16), ones[:, :], s1, start=False, stop=True).then_inc(pos_done, 1)

                    def gather(half, ready, onehot_value, done):
                        pe.wait_ge(ready, onehot_value)
                        for c in range(4):
                            for t in range(NT):
                                o = bank(6 + half, P, c * P)
                                vc = t * D + (4 * half + c) * P
                                TE.matmul(o, ahi[:, vc:vc + P], psel[:, t * P:(t + 1) * P], start=t == 0, stop=False)
                                last = TE.matmul(o, alo[:, vc:vc + P], psel[:, t * P:(t + 1) * P], start=False, stop=t == 1)
                        last.then_inc(done, 1)

                    def comb_transposed(done=ct_done, begun=None):
                        for t in range(NT):
                            last = TE.transpose(bank(5, P, t * P), wk(CPN + t * P, P), ident[:, :])
                            if t == 0 and begun is not None:
                                last.then_inc(begun, 1)
                        last.then_inc(done, 1)

                    def combine(q, t, done=combined):
                        for half in range(2):
                            last = TE.matmul(bank(6 + half), wk(CSB + q * 256 + t * P, P), wk(Y + half * 512, 512),
                                             start=True, stop=True)
                        last.then_inc(done, 1)

                    def transpose_ff(s):
                        for c in range(2):
                            last = TE.transpose(bank(4, P, c * P), wk(FFN_ + c * P, P), ident[:, :])
                        last.then_inc(m_tr, 1)

                    pe.wait_ge(v_lo, NT)
                    pe.wait_ge(onehot, 4)
                    comb_transposed()
                    for half in range(2):
                        gather(half, onehot, 4, gathered)
                    with pe.Fori(0, NE // 2) as it:
                        for q in range(2):
                            for k, (kind, j, part) in enumerate(ORDER):
                                m, s = q * PER_E + k, q * NS + j
                                n = (it, M0 + m)
                                if kind == "up":
                                    if k == 0:
                                        pe.wait_ge(xg_hi, it * 4 + 2 * q + 2)
                                        pe.wait_ge(xg_lo, it * 4 + 2 * q + 2)
                                    narrow(n, (M0 + m) % WR, XG + q * 1024, 4 * part, [bank(s % 2)], 512,
                                           a_pitch=P, first=part == 0, last=part == 1)
                                    if part == 0 and j > 0:
                                        pe.wait_ge(m_ff, it * (2 * NS) + s)
                                        if s >= 2:
                                            pe.wait_ge(m_tlo, it * (2 * NS) + s - 1)
                                        transpose_ff(s - 1)
                                else:
                                    def last_slice():
                                        pe.wait_ge(m_ff, it * (2 * NS) + s + 2)
                                        transpose_ff(s + 1)

                                    pe.wait_ge(m_thi, it * (2 * NS) + s + 1)
                                    pe.wait_ge(m_tlo, it * (2 * NS) + s + 1)
                                    if j == 0:
                                        pe.wait_ge(m_y, it * 2 + q + 1)
                                    wide_granule(n, (M0 + m) % WR, FFT + 256 * (s % 2), [(bank(2), bank(3))],
                                                 P, j == 0, j == NS - 1, last_slice if j == NS - 2 else None)
                                    if j in (2, 4):
                                        t = (j - 2) // 2
                                        if t == 1:
                                            pe.wait_ge(comb_added, it * 4 + 2 * q + 1)
                                        pe.wait_ge(xg_lo, it * 4 + 2 * q + 2)
                                        combine(1 - q, t)
                                    if j == 6:
                                        pe.wait_ge(onehot, it * 8 + 4 * q + 8)
                                        pe.wait_ge(ct_out, it * 2 + q + 1)
                                        comb_transposed()
                                    if j in (8, 9):
                                        if j == 8:
                                            pe.wait_ge(comb_added, it * 4 + 2 * q + 2)
                                        gather(j - 8, onehot, it * 8 + 4 * q + 8, gathered)
                    pe.wait_ge(m_y, NE + 1)
                    pe.wait_ge(xg_lo, 2 * NE + 2)
                    combine(1, 0)
                    pe.wait_ge(comb_added, 2 * NE + 1)
                    combine(1, 1)
                    with overflow(pe):
                        with pe.Fori(0, NE) as e:
                            pe.wait_ge(o_onehot, e * 4 + 4)
                            comb_transposed(o_ct, o_used)
                            for half in range(2):
                                gather(half, o_onehot, e * 4 + 4, o_gathered)
                            with pe.Fori(0, NS) as j:
                                pe.wait_ge(o_tokens, e * 2 + 2)
                                over = raw(RAW_MOE - 1)
                                for q in range(2):
                                    pe.wait_ge(o_landed, e * (96 * NS) + j * 96 + 32 * (q + 1))
                                    for c in range(4):
                                        last = TE.matmul(bank(0), wk(VO + (4 * q + c) * P, P),
                                                         over[:, c * 512:(c + 1) * 512],
                                                         start=q == 0 and c == 0, stop=q == 1 and c == 3)
                                    if q == 0:
                                        last.then_inc(o_used, 1)
                                last.then_inc(o_up, 1)
                                pe.wait_ge(o_ff, e * NS + j + 1)
                                for c in range(2):
                                    last = TE.transpose(bank(4, P, c * P), wk(FFN_ + c * P, P), ident[:, :])
                                    if c == 0:
                                        last.then_inc(o_used, 1)
                                last.then_inc(o_tr, 1)
                                pe.wait_ge(o_fft, e * NS + j + 1)
                                pe.wait_ge(o_landed, e * (96 * NS) + j * 96 + 96)
                                for half in range(2):
                                    for c in range(2):
                                        last = TE.matmul(bank(2 + half), wk(FFTO + c * P, P),
                                                         over[:, c * D + half * 512:c * D + half * 512 + 512],
                                                         start=c == 0, stop=c == 1)
                                last.then_inc(o_used, 1)
                            pe.wait_ge(o_y, e * NS + NS)
                            combine(0, 0, o_combined)
                            pe.wait_ge(o_added, e * 2 + 1)
                            combine(0, 1, o_combined)
                pe.wait_ge(p_landed, 16 * (layer + 1))
                for c in range(2):
                    for t in range(NT):
                        last = TE.transpose(bank(0, P, c * SEQ + t * P), wk(PNAT + t * PLE + c * P, P), ident[:, :])
                last.then_inc(pt_ready, 1)
                transpose_u(3 * layer + 2)
                wait_at()
                pe.wait_ge(pt_lo, layer + 1)
                first = base + G_PLE0 if layer == 0 else M0 + N_MOE
                for q in range(4):
                    if q % 2 == 0:
                        acc_free(layer, A_PLE + q // 2)
                    narrow(first + q, (first + q) % WR, 0, 4 * (q % 2), accs(layer, A_PLE + q // 2, 512), 512,
                           first=q % 2 == 0, last=q % 2 == 1)
                wide_granule(first + 4, (first + 4) % WR, 4096, [(bank(4), bank(5)), (bank(6), bank(7))], SEQ, True, True)



_INS = ["x", "p", "lb_param", "norm_mix", "w_in", "hg_onorm", "sa_cnorm", "sa_wk", "sa_wv", "w_branch", "w_out",
        "norm_ffn", "dense_wg", "dense_wu", "dense_wd", "moe_router", "moe_wg", "moe_wu", "moe_wd", "norm_ple",
        "ple_gate", "ple_proj", "norm_final"]


def kernel(**inputs):
    import numpy as _np
    import concourse.bacc as _bacc
    from concourse import mybir as _mybir
    from concourse.bass_utils import run_bass_kernel_spmd as _run

    nc = _bacc.Bacc("TRN2", target_bir_lowering=False, num_devices=1)
    arrays, args = {}, []
    for name in _INS:
        a = _np.ascontiguousarray(inputs[name])
        arrays[f"in_{name}"] = a
        args.append(nc.dram_tensor(f"in_{name}", a.shape, _mybir.dt.from_np(a.dtype), kind="ExternalInput").ap())
    args.append(nc.dram_tensor("out_h", (1, SEQ, D), _mybir.dt.float32, kind="ExternalOutput").ap())
    build(nc, *args)
    r = _run(nc, [arrays], core_ids=[0])
    return r.results[0]["out_h"]
```
